# Optimizing a Trainium2 kernel written in Bass

```python
import jax, jax.numpy as jnp
from jax import lax
import numpy as np

D_MODEL = 1024
BATCH = 1
SEQ = 512
DEPTH = 2
DEC_BATCH = 1
DEC_SEQ = 64
PAST_LEN = 128

CHUNK = 64
N_A = DEPTH // 2
N_B = DEPTH - N_A
RET_HEADS = 4
RET_DK = D_MODEL // RET_HEADS
RET_DV = 2 * RET_DK
RET_V = RET_HEADS * RET_DV
FOX_HEADS = 16
FOX_DH = D_MODEL // FOX_HEADS
FOX_W = FOX_HEADS * FOX_DH
D_FF = 2816
Q_BLOCK = 128
ROPE_BASE = 10000.0
EPS = 1e-6

kernel_name = "yoco_retention_fox_macaron_stream"

def rmsnorm(x, g):
    xf = x.astype(jnp.float32)
    y = xf * lax.rsqrt(jnp.mean(xf * xf, axis=-1, keepdims=True) + EPS) * g.astype(jnp.float32)
    return y.astype(x.dtype)

def swiglu_ffn(h, g, w_in, w_out):
    gate, up = jnp.split(rmsnorm(h, g) @ w_in, 2, axis=-1)
    return (jax.nn.silu(gate) * up) @ w_out

def rope(x, pos):
    half = x.shape[-1] // 2
    inv = ROPE_BASE ** (-jnp.arange(half, dtype=jnp.float32) / half)
    ang = pos.astype(jnp.float32)[:, None] * inv[None, :]
    cos, sin = jnp.cos(ang)[None, :, None, :], jnp.sin(ang)[None, :, None, :]
    xf = x.astype(jnp.float32)
    x1, x2 = xf[..., :half], xf[..., half:]
    return jnp.concatenate([x1 * cos - x2 * sin, x1 * sin + x2 * cos], axis=-1)

def retention_log_gamma():
    return jnp.log1p(-jnp.exp2(-5.0 - jnp.arange(RET_HEADS, dtype=jnp.float32)))

def retention_chunk(S, q, k, v, log_gamma):
    c = q.shape[1]
    pos = jnp.arange(c, dtype=jnp.float32)
    dist = jnp.abs(pos[:, None] - pos[None, :])
    decay_intra = jnp.exp(log_gamma[:, None, None] * dist)
    scores = jnp.einsum('bchd,bshd->bhcs', q, k) * decay_intra[None]
    intra = jnp.einsum('bhcs,bshe->bche', scores, v)
    q_decay = jnp.exp(log_gamma[None, :] * (pos[:, None] + 1.0))
    inter = jnp.einsum('bchd,bhde->bche', q, S) * q_decay[None, :, :, None]
    k_decay = jnp.exp(log_gamma[None, :] * (c - 1.0 - pos[:, None]))
    S_new = jnp.exp(log_gamma * c)[None, :, None, None] * S + jnp.einsum(
        'bchd,bche->bhde', k * k_decay[None, :, :, None], v)
    return S_new, intra + inter

def retention_mixer(h, S0, pos, chunk_len, w_in, gn_g, w_out):
    B, L, _ = h.shape
    q, k, v, g = jnp.split(h @ w_in, [D_MODEL, 2 * D_MODEL, 2 * D_MODEL + RET_V], axis=-1)
    q = rope(q.reshape(B, L, RET_HEADS, RET_DK), pos) * (RET_DK ** -0.5)
    k = rope(k.reshape(B, L, RET_HEADS, RET_DK), pos)
    v = v.reshape(B, L, RET_HEADS, RET_DV).astype(jnp.float32)
    n = L // chunk_len
    to_chunks = lambda t: jnp.moveaxis(t.reshape(B, n, chunk_len, *t.shape[2:]), 1, 0)
    log_gamma = retention_log_gamma()
    S_fin, o = lax.scan(lambda S, qkv: retention_chunk(S, qkv[0], qkv[1], qkv[2], log_gamma),
                        S0.astype(jnp.float32), (to_chunks(q), to_chunks(k), to_chunks(v)))
    o = jnp.moveaxis(o, 0, 1).reshape(B, L, RET_HEADS, RET_DV)
    mu = jnp.mean(o, axis=-1, keepdims=True)
    var = jnp.mean(jnp.square(o - mu), axis=-1, keepdims=True)
    o = ((o - mu) * lax.rsqrt(var + EPS)).reshape(B, L, RET_V) * gn_g.astype(jnp.float32)
    o = (jax.nn.silu(g.astype(jnp.float32)) * o).astype(h.dtype)
    return o @ w_out, S_fin

def fox_kv(h, kv_g, w_kvf, b_f):
    B, L, _ = h.shape
    k, v, fl = jnp.split(rmsnorm(h, kv_g) @ w_kvf, [FOX_W, 2 * FOX_W], axis=-1)
    logf = jax.nn.log_sigmoid(fl.astype(jnp.float32) + b_f.astype(jnp.float32))
    return (k.reshape(B, L, FOX_HEADS, FOX_DH), v.reshape(B, L, FOX_HEADS, FOX_DH), logf)

def fox_block(q_blk, c_blk, qpos, k, v, cumf, kpos):
    s = jnp.einsum('bqhd,bkhd->bhqk', q_blk, k).astype(jnp.float32) * (FOX_DH ** -0.5)
    s = s + jnp.swapaxes(c_blk, 1, 2)[..., None] - jnp.swapaxes(cumf, 1, 2)[:, :, None, :]
    s = jnp.where((qpos[:, None] >= kpos[None, :])[None, None], s, -jnp.inf)
    p = jax.nn.softmax(s, axis=-1)
    return jnp.einsum('bhqk,bkhd->bqhd', p.astype(v.dtype), v)

def fox_mixer(h, w_q, w_out, k, v, cumf, kpos, qpos, c_q):
    B, L, _ = h.shape
    q = (h @ w_q).reshape(B, L, FOX_HEADS, FOX_DH)
    nb = max(L // Q_BLOCK, 1)
    qb = L // nb
    blocks = (jnp.moveaxis(q.reshape(B, nb, qb, FOX_HEADS, FOX_DH), 1, 0),
              jnp.moveaxis(c_q.reshape(B, nb, qb, FOX_HEADS), 1, 0),
              qpos.reshape(nb, qb))
    o = lax.map(lambda a: fox_block(a[0], a[1], a[2], k, v, cumf, kpos), blocks)
    o = jnp.moveaxis(o, 0, 1).reshape(B, L, FOX_W)
    return o @ w_out

def trunk(x, pos, chunk_len, ret_S0, past, p):
    h = x
    L = x.shape[1]
    ret_states = []
    k_new = v_new = logf_new = None
    k_all = v_all = cumf_all = kpos = c_q = None
    for layer in range(DEPTH):
        h = h + 0.5 * swiglu_ffn(h, p['ffn1_g'][layer], p['ffn1_w_in'][layer], p['ffn1_w_out'][layer])
        hn = rmsnorm(h, p['mix_g'][layer])
        if layer < N_A:
            y, S = retention_mixer(hn, ret_S0[layer], pos, chunk_len,
                                   p['ret_w_in'][layer], p['ret_gn_g'][layer], p['ret_w_out'][layer])
            ret_states.append(S)
        else:
            j = layer - N_A
            y = fox_mixer(hn, p['fox_w_q'][j], p['fox_w_out'][j], k_all, v_all, cumf_all, kpos, pos, c_q)
        h = h + y
        h = h + 0.5 * swiglu_ffn(h, p['ffn2_g'][layer], p['ffn2_w_in'][layer], p['ffn2_w_out'][layer])
        if layer == N_A - 1:
            k_new, v_new, logf_new = fox_kv(h, p['kv_g'], p['fox_w_kvf'], p['fox_b_f'])
            if past is None:
                k_all, v_all, logf_all = k_new, v_new, logf_new
            else:
                k_all = jnp.concatenate([past[0].astype(k_new.dtype), k_new], axis=1)
                v_all = jnp.concatenate([past[1].astype(v_new.dtype), v_new], axis=1)
                logf_all = jnp.concatenate([past[2].astype(jnp.float32), logf_new], axis=1)
            cumf_all = jnp.cumsum(logf_all, axis=1)
            n_keys = k_all.shape[1]
            kpos = jnp.arange(n_keys)
            c_q = cumf_all[:, n_keys - L:]
    return (rmsnorm(h, p['final_g']), jnp.stack(ret_states), k_new, v_new, logf_new)

def setup_inputs(seed: int = 0) -> dict:
    key = jax.random.key(seed)
    ks = jax.random.split(key, 24)
    nrm = lambda k, shape, scale: jax.random.normal(k, shape, jnp.float32) * scale
    gain = lambda k, shape: 1.0 + 0.05 * jax.random.normal(k, shape, jnp.float32)
    return {
        'x_prompt': nrm(ks[0], (BATCH, SEQ, D_MODEL), 1.0),
        'x_sample': nrm(ks[1], (DEC_BATCH, DEC_SEQ, D_MODEL), 1.0),
        'state_ret': nrm(ks[2], (N_A, DEC_BATCH, RET_HEADS, RET_DK, RET_DV), 0.1),
        'cache_k': nrm(ks[3], (DEC_BATCH, PAST_LEN, FOX_HEADS, FOX_DH), 1.0),
        'cache_v': nrm(ks[4], (DEC_BATCH, PAST_LEN, FOX_HEADS, FOX_DH), 1.0),
        'cache_logf': jax.nn.log_sigmoid(3.0 + nrm(ks[5], (DEC_BATCH, PAST_LEN, FOX_HEADS), 1.0)),
        'ffn1_g': gain(ks[6], (DEPTH, D_MODEL)),
        'ffn1_w_in': nrm(ks[7], (DEPTH, D_MODEL, 2 * D_FF), D_MODEL ** -0.5),
        'ffn1_w_out': nrm(ks[8], (DEPTH, D_FF, D_MODEL), D_FF ** -0.5),
        'mix_g': gain(ks[9], (DEPTH, D_MODEL)),
        'ffn2_g': gain(ks[10], (DEPTH, D_MODEL)),
        'ffn2_w_in': nrm(ks[11], (DEPTH, D_MODEL, 2 * D_FF), D_MODEL ** -0.5),
        'ffn2_w_out': nrm(ks[12], (DEPTH, D_FF, D_MODEL), D_FF ** -0.5),
        'ret_w_in': nrm(ks[13], (N_A, D_MODEL, 2 * D_MODEL + 2 * RET_V), D_MODEL ** -0.5),
        'ret_gn_g': gain(ks[14], (N_A, RET_V)),
        'ret_w_out': nrm(ks[15], (N_A, RET_V, D_MODEL), RET_V ** -0.5),
        'kv_g': gain(ks[16], (D_MODEL,)),
        'fox_w_kvf': nrm(ks[17], (D_MODEL, 2 * FOX_W + FOX_HEADS), D_MODEL ** -0.5),
        'fox_b_f': jnp.linspace(1.0, 5.0, FOX_HEADS, dtype=jnp.float32) + nrm(ks[18], (FOX_HEADS,), 0.1),
        'fox_w_q': nrm(ks[19], (N_B, D_MODEL, FOX_W), D_MODEL ** -0.5),
        'fox_w_out': nrm(ks[20], (N_B, FOX_W, D_MODEL), FOX_W ** -0.5),
        'final_g': gain(ks[21], (D_MODEL,)),
    }

def reference(x_prompt, x_sample, state_ret, cache_k, cache_v, cache_logf,
              ffn1_g, ffn1_w_in, ffn1_w_out, mix_g, ffn2_g, ffn2_w_in, ffn2_w_out,
              ret_w_in, ret_gn_g, ret_w_out, kv_g, fox_w_kvf, fox_b_f, fox_w_q, fox_w_out, final_g):
    p = {'ffn1_g': ffn1_g, 'ffn1_w_in': ffn1_w_in, 'ffn1_w_out': ffn1_w_out, 'mix_g': mix_g,
         'ffn2_g': ffn2_g, 'ffn2_w_in': ffn2_w_in, 'ffn2_w_out': ffn2_w_out,
         'ret_w_in': ret_w_in, 'ret_gn_g': ret_gn_g, 'ret_w_out': ret_w_out,
         'kv_g': kv_g, 'fox_w_kvf': fox_w_kvf, 'fox_b_f': fox_b_f,
         'fox_w_q': fox_w_q, 'fox_w_out': fox_w_out, 'final_g': final_g}
    b_p, l_p = x_prompt.shape[0], x_prompt.shape[1]
    l_s = x_sample.shape[1]
    past_len = cache_k.shape[1]
    S0_prompt = jnp.zeros((N_A, b_p, RET_HEADS, RET_DK, RET_DV), jnp.float32)
    y_prompt, state_ret_prompt, k_prompt, v_prompt, logf_prompt = trunk(
        x_prompt, jnp.arange(l_p), CHUNK, S0_prompt, None, p)
    y_sample, state_ret_sample, k_sample, v_sample, logf_sample = trunk(
        x_sample, past_len + jnp.arange(l_s), l_s, state_ret, (cache_k, cache_v, cache_logf), p)
    return (y_prompt, y_sample, state_ret_prompt, k_prompt, v_prompt, logf_prompt,
            state_ret_sample, k_sample, v_sample, logf_sample)


_drawn_inputs = setup_inputs


def setup_inputs(seed=0):
    import zlib

    import numpy as np

    out = dict(_drawn_inputs(seed))
    spreads = {}
    factors = {'state_ret': 6.378, 'cache_logf': 4.347}
    for name, (base, spread) in spreads.items():
        noise = np.random.default_rng([zlib.crc32(name.encode()), seed]).standard_normal(out[name].shape)
        drawn = base * np.exp(spread * noise) if base else spread * noise
        out[name] = __import__('jax').numpy.asarray(drawn.astype(out[name].dtype))
    for name, factor in factors.items():
        out[name] = (out[name] * factor).astype(out[name].dtype)
    return out
```

```python
from contextlib import ExitStack

import numpy as np

import concourse.bass as bass
from concourse import mybir

F32 = mybir.dt.float32
F32R = mybir.dt.float32r
BF16 = mybir.dt.bfloat16
I32 = mybir.dt.int32
ALU = mybir.AluOpType
ACT = mybir.ActivationFunctionType
AX_X = mybir.AxisListType.X

P = 128
D = 1024
KD = D // P
TP, TS = 512, 64
T = TP + TS
HT = T // 2
PAST = 128
FF = 2816
KF = FF // P
FF_PARTS = [(0, 12), (12, 10)]
HEADS = 4
DK, DV = D // HEADS, 2 * D // HEADS
CHUNK = 64
FOX_HEADS = 16
PAIRS = FOX_HEADS // 2
EPS = 1e-6
RAW, SPLIT = 4, 2
KMAX = 12
TT = 5
ROWS = [P, P, P, P, TS]
KEYS = [128 * (i + 1) for i in range(4)]
SOFF = [0, 128, 384, 768]
PTOFF = [0, 512, 1024, 896]
S_BANK = [(0, 0), (1, 0), (0, 128), (2, 0)]
STOFF = [0, 512, 896, 1152]
O_BANK = [5, 6, 7, 4, 5]
GN_STEPS = 2 * TT + 3 + 3 * 3
PAIR_LOADS = 9
NEG = -1e30
LEAST = -3e38
RSQRT_SEED = 1597463007.0

C_COS, C_SIN, C_ID, C_TRI, C_TRIS = 0, T, 2 * T, 2 * T + P, 2 * T + 2 * P
C_QDEC = C_TRIS + TS
C_KDEC = C_QDEC + HEADS * TS
C_GCH = C_KDEC + HEADS * TT
C_ALL = C_GCH + HEADS

G_FFN1, G_MIX, G_FFN2, G_KV, G_FIN, G_GN = 0, 16, 32, 48, 56, 64
G_ALL = 80


def constant_tables():
    pos = np.concatenate([np.arange(TP), PAST + np.arange(TS)]).astype(np.float32)
    half = DK // 2
    inv = (np.float32(10000.0) ** (-np.arange(half, dtype=np.float32) / np.float32(half))).astype(np.float32)
    ang = (pos[None, :] * inv[:, None]).astype(np.float32).astype(np.float64)
    lg = np.log1p(-np.exp2(-5.0 - np.arange(HEADS)))
    c = np.zeros((P, C_ALL), np.float32)
    c[:, C_COS:C_COS + T] = np.cos(ang)
    c[:, C_SIN:C_SIN + T] = np.sin(ang)
    c[:, C_ID:C_ID + P] = np.eye(P)
    p = np.arange(P)
    c[:, C_TRI:C_TRI + P] = np.where(p[None, :] > p[:, None], NEG, 0.0)
    c[:, C_TRIS:C_TRIS + TS] = np.where(np.arange(TS)[None, :] > (p % TS)[:, None], NEG, 0.0)
    mask = np.zeros((HEADS, P, TP), np.float32)
    i, j = np.arange(TP)[None, :], p[:, None]
    for h in range(HEADS):
        c[:, C_QDEC + h * TS:C_QDEC + (h + 1) * TS] = np.exp(lg[h] * (np.arange(TS) + 1.0))[None, :]
        for t in range(4):
            c[:, C_KDEC + h * TT + t] = np.exp(lg[h] * (TP - 1.0 - (t * P + p)))
        c[:, C_KDEC + h * TT + 4] = np.exp(lg[h] * np.maximum(CHUNK - 1.0 - p, 0.0))
        c[:, C_GCH + h] = np.exp(lg[h] * CHUNK)
        mask[h] = np.where(i // CHUNK >= j // CHUNK, np.exp(lg[h] * np.abs(i - j)), 0.0)
    return c, mask


def encoder(nc, A, O):
    sections = []
    def ffn_sections(name):
        for part, (_, n) in enumerate(FF_PARTS):
            sections.append((f"{name}_in{part}", 2 * n, KD))
            sections.append((f"{name}_out{part}", KD, n))
    ffn_sections("ffn1_0")
    sections.append(("ret", 20 * HEADS, KD))
    ffn_sections("ffn2_0")
    sections += [("k", KD, KD), ("v", KD, KD)]
    ffn_sections("ffn1_1")
    sections += [("q", KD, KD), ("fox_out", KD, KD)]
    ffn_sections("ffn2_1")
    first, units_of, blocks, following, at = {}, {}, {}, {}, 0
    for n, (name, units, kt) in enumerate(sections):
        assert units % 4 == 0
        first[name], units_of[name], blocks[name] = at, units, kt
        following[name] = sections[n + 1][2] if n + 1 < len(sections) else None
        at += units
    RET = first["ret"]

    with ExitStack() as ctx:
        def sem(name):
            return ctx.enter_context(nc.semaphore(name))

        base = nc.sbuf_base + (-nc.sbuf_base) % 64
        place = {"fixed": base}

        def sb(region, name, shape, dt=F32):
            size = int(np.prod(shape[1:])) * mybir.dt.size(dt)
            off = place[region]
            place[region] = off + size + (-size) % 32
            assert place[region] <= nc.sbuf_usable_end, (name, place[region])
            return nc.alloc_sbuf_tensor_at(name, list(shape), dt, offset=off)

        h = sb("fixed", "h", [P, KD, T])
        xh = sb("fixed", "xh", [P, KD, T], F32R)
        xl = sb("fixed", "xl", [P, KD, T], F32R)
        raw = sb("fixed", "raw", [P, RAW, KMAX, P])
        wh = sb("fixed", "wh", [P, SPLIT, KMAX, P], F32R)
        wl = sb("fixed", "wl", [P, SPLIT, KMAX, P], F32R)
        rstd = sb("fixed", "rstd", [P, T])
        newt = sb("fixed", "newt", [P, T])
        ssq = sb("fixed", "ssq", [P, T])
        sq = sb("fixed", "sq", [P, T])
        const = sb("fixed", "const", [P, C_ALL])
        ones = sb("fixed", "ones", [P, P])
        gains = sb("fixed", "gains", [P, G_ALL])
        bf = sb("fixed", "bf", [FOX_HEADS, 1])
        idb = sb("fixed", "idb", [P, P], BF16)
        trib = sb("fixed", "trib", [P, P], BF16)
        trisb = sb("fixed", "trisb", [P, TS], BF16)
        scrap = sb("fixed", "scrap", [P, 1])
        ident = const[:, C_ID:C_ID + P]

        for region in ("ffn", "ret", "kv", "fox", "io"):
            place[region] = place["fixed"]
        acth = sb("ffn", "acth", [P, KMAX, T], F32R)
        actl = sb("ffn", "actl", [P, KMAX, T], F32R)
        gate = sb("ffn", "gate", [P, 2, T])
        silu = sb("ffn", "silu", [P, 2, T])
        rsilu = sb("ffn", "rsilu", [P, 2, T])
        prod = sb("ffn", "prod", [P, 2, T])

        qk = sb("ret", "qk", [P, 4, T])
        gT = sb("ret", "gT", [P, 4, T])
        vtok = sb("ret", "vtok", [P, TT, DV])
        ktok = sb("ret", "ktok", [P, TT, DK])
        place["ret_late"] = place["ret"]
        sT = sb("ret", "sT", [P, 1280 + TS])
        sp_out = sb("ret_late", "sp_out", [P, 2, DV])
        ogh = sb("ret", "ogh", [P, 4, T], F32R)
        ogl = sb("ret", "ogl", [P, 4, T], F32R)
        place["ret_early"] = place["ret"]
        vT = sb("ret_early", "vT", [P, 4, T])
        otok = sb("ret", "otok", [P, TT, DV])
        place["ret"] = max(place["ret"], place["ret_early"])
        rt = sb("ret", "rt", [P, 6, T])
        ogt = rt[:, 0:2, :]
        dm = sb("ret", "dm", [P, TP])
        s0 = sb("ret", "s0", [P, 2, DV])
        qd = sb("ret", "qd", [P, 2, TS])
        bst = sb("ret", "bst", [P, TT, 6])
        mv = sb("ret", "mv", [P, TT, 2])
        gx = sb("ret", "gx", [P, TT])
        gy = sb("ret", "gy", [P, TT])
        ga = sb("ret", "ga", [P, TT])

        kvt = sb("kv", "kvt", [P, 2, T])
        kvtok = sb("kv", "kvtok", [P, 2, TT, P])
        fw = sb("kv", "fw", [P, KD, FOX_HEADS])
        fwp = sb("kv", "fwp", [P, KD, P])
        fwh = sb("kv", "fwh", [P, KD, P], F32R)
        fwl = sb("kv", "fwl", [P, KD, P], F32R)
        lz, la, le, ls, lp, lm, logf = [sb("kv", n, [FOX_HEADS, T]) for n in ("lz", "la", "le", "ls", "lp", "lm", "logf")]
        cumf = sb("kv", "cumf", [FOX_HEADS, T + PAST])
        ones_row = sb("kv", "ones_row", [FOX_HEADS, TP])
        clf = sb("kv", "clf", [P, FOX_HEADS])
        catf = sb("kv", "catf", [FOX_HEADS, PAST + TS])
        ftok = sb("kv", "ftok", [P, TT, FOX_HEADS])

        qT = sb("fox", "qT", [P, PAIRS, T])
        kTp = sb("fox", "kTp", [P, 2, T])
        ckp = sb("fox", "ckp", [P, 2, P])
        kTc = sb("fox", "kTc", [P, 2, P])
        vp = sb("fox", "vp", [P, 2, 6, P])
        bias = sb("fox", "bias", [P, 2, 2, TP])
        bias_s = sb("fox", "bias_s", [P, 2, PAST + TS])
        sc = sb("fox", "sc", [P, 2, 1280])
        sc_s = sb("fox", "sc_s", [P, PAST + TS])
        pt = sb("fox", "pt", [P, 2, 1280])
        pts = sb("fox", "pts", [P, 2, P])
        qpad = sb("fox", "qpad", [P, 2, 2, TP])
        qpad_s = sb("fox", "qpad_s", [P, 2, P])
        mx, nmx, rsum, rinv = [sb("fox", n, [P, 2, 5]) for n in ("mx", "nmx", "rsum", "rinv")]

        xtok = sb("io", "xtok", [P, TT, D])
        grow = sb("io", "grow", [G_ALL, P])
        yT = sb("io", "yT", [P, KD, T])
        ytok = sb("io", "ytok", [P, TT, D])

        ps = ctx.enter_context(nc.psum_tensor("ps", [P, 8, 512], F32))

        def unit_psum(s):
            return ps[:, 2 * (s % 2):2 * (s % 2) + 2, 0:HT]

        def halves(ap):
            return ap.rearrange("p (a t) -> p a t", a=2)

        kT_dram = nc.dram_tensor("kT_scratch", (D, T), F32, kind="Internal").ap()
        cum_dram = nc.dram_tensor("cum_scratch", (FOX_HEADS, T + PAST), F32, kind="Internal").ap()

        raw_ready = [sem(f"raw_ready{i}") for i in range(RAW)]
        hi_ready = sem("hi_ready")
        lo_ready = sem("lo_ready")
        unit_done = sem("unit_done")
        taken = sem("taken")
        const_in = sem("const_in")
        x_in = sem("x_in")
        setup = sem("setup")
        gt_ready = sem("gt_ready")
        gains_ready = sem("gains_ready")
        xt_ready = sem("xt_ready")
        h0_ready = sem("h0_ready")
        xhi_ready = sem("xhi_ready")
        x_ready = sem("x_ready")
        sq_step = sem("sq_step")
        ssq_ready = sem("ssq_ready")
        msum_ready = sem("msum_ready")
        newton = sem("newton")
        rstd_ready = sem("rstd_ready")
        silu_ready = sem("silu_ready")
        rsilu_ready = sem("rsilu_ready")
        act_hi = sem("act_hi")
        act_ready = sem("act_ready")

        head_in = sem("head_in")
        rope_mul = sem("rope_mul")
        rope_dve = sem("rope_dve")
        rope_pmul = sem("rope_pmul")
        rope_pool = sem("rope_pool")
        gT_ready = sem("gT_ready")
        qd_ready = sem("qd_ready")
        vt_done = sem("vt_done")
        kt_done = sem("kt_done")
        vtok_ready = sem("vtok_ready")
        ktok_ready = sem("ktok_ready")
        s_done = sem("s_done")
        sT_ready = sem("sT_ready")
        o_done = sem("o_done")
        otok_ready = sem("otok_ready")
        gn_step = sem("gn_step")
        on_ready = sem("on_ready")
        sp_done = sem("sp_done")
        sp_copied = sem("sp_copied")
        sn_done = sem("sn_done")
        sn_ready = sem("sn_ready")
        ot_done = sem("ot_done")
        ogt_ready = sem("ogt_ready")
        ogh_ready = sem("ogh_ready")
        og_ready = sem("og_ready")
        sp_stored = sem("sp_stored")
        sn_stored = sem("sn_stored")

        kvt_done = sem("kvt_done")
        kvtok_ready = sem("kvtok_ready")
        kT_stored = [sem(f"kT_stored{i}") for i in range(2)]
        kv_stored = [sem(f"kv_stored{i}") for i in range(2)]
        fw_in = sem("fw_in")
        fwp_ready = sem("fwp_ready")
        fwh_ready = sem("fwh_ready")
        fw_ready = sem("fw_ready")
        f_done = sem("f_done")
        gate_step = sem("gate_step")
        exp_ready = sem("exp_ready")
        logf_ready = sem("logf_ready")
        ft_done = sem("ft_done")
        ftok_ready = sem("ftok_ready")
        cum_ready = sem("cum_ready")
        f_stored = sem("f_stored")
        cum_stored = sem("cum_stored")

        pair_in = [sem(f"pair_in{i}") for i in range(2)]
        pad_zero = sem("pad_zero")
        qpad_ready = sem("qpad_ready")
        ckt_done = sem("ckt_done")
        kTc_ready = sem("kTc_ready")
        qk_done = sem("qk_done")
        scrapped = sem("scrapped")
        max_ready = sem("max_ready")
        nmx_ready = sem("nmx_ready")
        exp_done = sem("exp_done")
        rinv_ready = sem("rinv_ready")
        p_ready = sem("p_ready")
        pt_done = sem("pt_done")
        pt_act = sem("pt_act")
        pt_dve = sem("pt_dve")
        av_done = sem("av_done")
        foxh_ready = sem("foxh_ready")
        fox_ready = sem("fox_ready")

        y_ready = sem("y_ready")
        yt_done = sem("yt_done")
        ytok_act = sem("ytok_act")
        ytok_dve = sem("ytok_dve")
        y_stored = sem("y_stored")

        block = ctx.enter_context(nc.Block())

        def apart(eng):
            eng.wait_ge(setup, 1)

        @block.sync
        def _(sp):
            def load(u, s, src, kt):
                if not (isinstance(u, int) and u < RAW):
                    sp.wait_ge(lo_ready, u - RAW + 1)
                sp.dma_start(raw[:, s % RAW, 0:kt, :], src).then_inc(raw_ready[s % RAW], 16)

            def tiles_of(w):
                return w.rearrange("(k p) (j n) -> j p k n", p=P, n=P)

            def ffn(w_in, w_out, name):
                w_in, w_out = tiles_of(w_in), tiles_of(w_out)
                for part, (j0, n) in enumerate(FF_PARTS):
                    u0, u1 = first[f"{name}_in{part}"], first[f"{name}_out{part}"]

                    def two_pairs(i):
                        for s in range(4):
                            load(u0 + 4 * i + s, s, w_in[j0 + 2 * i + s // 2 + KF * (s % 2)], KD)
                    if u0 == 0:
                        two_pairs(0)
                    with sp.Fori(int(u0 == 0), n // 2) as i:
                        two_pairs(i)
                    with sp.Fori(0, 2) as i:
                        for s in range(4):
                            load(u1 + 4 * i + s, s, w_out[4 * i + s][:, j0:j0 + n, :], n)

            def plain(w, name):
                with sp.Fori(0, 2) as i:
                    for s in range(4):
                        load(first[name] + 4 * i + s, s, w[4 * i + s], KD)

            sp.dma_start(xtok[:, 0:4, :], A["x_prompt"][0].rearrange("(i p) d -> p i d", p=P)).then_inc(x_in, 16)
            sp.dma_start(xtok[0:TS, 4, :], A["x_sample"][0]).then_inc(x_in, 16)
            sp.dma_start(const[:, :], A["tables"]).then_inc(const_in, 16)
            for g0, name in ((G_FFN1, "ffn1_g"), (G_MIX, "mix_g"), (G_FFN2, "ffn2_g"), (G_GN, "ret_gn_g")):
                sp.dma_start(grow[g0:g0 + 16, :], A[name].rearrange("l (k p) -> (l k) p", p=P)).then_inc(const_in, 16)
            for g0, name in ((G_KV, "kv_g"), (G_FIN, "final_g")):
                sp.dma_start(grow[g0:g0 + 8, :], A[name].rearrange("(k p) -> k p", p=P)).then_inc(const_in, 16)
            sp.dma_start(bf[:, :], A["fox_b_f"].rearrange("(h a) -> h a", a=1)).then_inc(const_in, 16)

            ffn(A["ffn1_w_in"][0], A["ffn1_w_out"][0], "ffn1_0")
            ret_in = tiles_of(A["ret_w_in"][0])
            ret_out = A["ret_w_out"][0].rearrange("(h k p) (j n) -> h j p k n", p=P, k=4, n=P)
            with sp.Fori(0, HEADS) as hd:
                tiles = [c0 + w * hd + c for c0, w in ((0, 2), (KD, 2), (2 * KD, 4), (4 * KD, 4)) for c in range(w)]
                for s, j in enumerate(tiles):
                    load(RET + 20 * hd + s, s, ret_in[j], KD)
                for j in range(KD):
                    load(RET + 20 * hd + 12 + j, j, ret_out[hd, j], 4)
            ffn(A["ffn2_w_in"][0], A["ffn2_w_out"][0], "ffn2_0")
            plain(tiles_of(A["fox_w_kvf"][:, 0:D]), "k")
            plain(tiles_of(A["fox_w_kvf"][:, D:2 * D]), "v")
            ffn(A["ffn1_w_in"][1], A["ffn1_w_out"][1], "ffn1_1")
            plain(tiles_of(A["fox_w_q"][0]), "q")

            for n in range(2):
                sp.wait_ge(kT_stored[n], 16 * KD // 2)
                sp.wait_ge(kv_stored[n], 32 * KD)
            sp.wait_ge(cum_stored, 16)
            sp.wait_ge(unit_done, first["q"])
            new_keys = kT_dram.rearrange("(t p) n -> t p n", p=P)
            old_keys = A["cache_k"][0].rearrange("n (t e) d -> t n (e d)", e=2)
            old_values = A["cache_v"][0].rearrange("n (t e) d -> t n (e d)", e=2)
            prompt_values = O["v_prompt"][0].rearrange("(i p) (t e) d -> t p i (e d)", p=P, e=2)
            sample_values = O["v_sample"][0].rearrange("n (t e) d -> t n (e d)", e=2)
            sums = cum_dram.rearrange("(t e) n -> t e n", e=2)

            def pair(t, b):
                got = pair_in[b]
                sp.dma_start(kTp[:, b, :], new_keys[t]).then_inc(got, 16)
                sp.dma_start(ckp[:, b, :], old_keys[t]).then_inc(got, 16)
                for e in range(2):
                    sp.dma_start(bias[:, b, e, :], sums[t][e:e + 1, 0:TP].to_broadcast((P, TP))).then_inc(got, 16)
                    sp.dma_start(bias_s[TS * e:TS * e + TS, b, :],
                                 sums[t][e:e + 1, TP:].to_broadcast((TS, PAST + TS))).then_inc(got, 16)
                sp.dma_start(vp[:, b, 0:4, :], prompt_values[t]).then_inc(got, 16)
                sp.dma_start(vp[0:TS, b, 4, :], sample_values[t]).then_inc(got, 16)
                sp.dma_start(vp[:, b, 5, :], old_values[t]).then_inc(got, 16)
            pair(0, 0)
            pair(1, 1)
            out_w = tiles_of(A["fox_w_out"][0])
            for s in range(4):
                load(first["fox_out"] + s, s, out_w[s], KD)
            with sp.Fori(1, PAIRS // 2) as i:
                for b in range(2):
                    sp.wait_ge(av_done, 3 * (2 * i + b - 1))
                    pair(2 * i + b, b)
            for s in range(4):
                load(first["fox_out"] + 4 + s, s, out_w[4 + s], KD)
            ffn(A["ffn2_w_in"][1], A["ffn2_w_out"][1], "ffn2_1")

        def split_hi(act, u, q, s, kt):
            act.wait_ge(raw_ready[s], 16 * q + 16)
            if not (isinstance(u, int) and u < SPLIT):
                act.wait_ge(unit_done, u - SPLIT + 1)
            nc.scalar.copy(wh[:, s % SPLIT, 0:kt, :], raw[:, s, 0:kt, :]).then_inc(hi_ready, 1)

        def split_lo(dve, u, q, s, kt):
            dve.wait_ge(hi_ready, u + 1)
            nc.vector.tensor_tensor(wl[:, s % SPLIT, 0:kt, :], raw[:, s, 0:kt, :],
                                    wh[:, s % SPLIT, 0:kt, :].bitcast(F32), ALU.subtract).then_inc(lo_ready, 1)

        def section(eng, name, split, take, after_first=None):
            u0, n4 = first[name], units_of[name] // 4

            def four(i, last=False, start=False):
                for s in range(4):
                    a = s + 2
                    kt = following[name] if last and a >= 4 else blocks[name]
                    if kt is not None:
                        split(eng, u0 + 4 * i + a, u0 // 4 + i + a // 4, a % 4, kt)
                    if start and s == 0 and after_first is not None:
                        after_first()
                    take(i, s)
            four(0, start=True)
            if n4 > 2:
                with eng.Fori(1, n4 - 1) as i:
                    four(i)
            four(n4 - 1, last=True)

        @block.scalar
        def _(act):
            n_x = [0]

            def x_tile(j, gain):
                n_x[0] += 1
                nc.scalar.activation(xh[:, j, :], h[:, j, :], ACT.Copy, scale=gains[:, gain + j:gain + j + 1]) \
                    .then_inc(xhi_ready, 1)

            def ffn(name, gain):
                for part, (j0, n) in enumerate(FF_PARTS):
                    u0, u1 = first[f"{name}_in{part}"], first[f"{name}_out{part}"]

                    def take_in(i, s):
                        act.wait_ge(taken, u0 + 4 * i + s + 1)
                        if s % 2 == 0:
                            nc.scalar.activation(silu[:, s // 2, :], gate[:, s // 2, :], ACT.Silu).then_inc(silu_ready, 1)
                        else:
                            nc.scalar.copy(acth[:, 2 * i + s // 2, :], prod[:, s // 2, :]).then_inc(act_hi, 1)

                    def take_out(i, s):
                        if part == 1 and gain is not None:
                            act.wait_ge(taken, u1 + 4 * i + s + 1)
                            x_tile(4 * i + s, gain)
                    section(act, f"{name}_in{part}", split_hi, take_in)
                    section(act, f"{name}_out{part}", split_hi, take_out)

            act.wait_ge(gt_ready, 1)
            nc.scalar.copy(gains[:, :], ps[:, 3, 0:G_ALL]).then_inc(gains_ready, 1)
            act.wait_ge(gains_ready, 1)
            split_hi(act, 0, 0, 0, KD)
            split_hi(act, 1, 0, 1, KD)
            for j in range(KD):
                act.wait_ge(h0_ready, 2 * j + 2)
                x_tile(j, G_FFN1)
            ffn("ffn1_0", G_MIX)

            def head(hd, last):
                u0, q0 = RET + 20 * hd, RET // 4 + 5 * hd
                for s in range(12):
                    a = s + 2
                    split_hi(act, u0 + a, q0 + a // 4, a % 4, KD if a < 12 else 4)
                for t in range(TT):
                    act.wait_ge(vt_done, TT * hd + t + 1)
                    nc.scalar.copy(vtok[0:ROWS[t], t, :], ps[0:ROWS[t], 4 + t % 2, :]).then_inc(vtok_ready, 1)
                act.wait_ge(taken, u0 + 12)
                for f in range(4):
                    nc.scalar.activation(gT[:, f, :], gT[:, f, :], ACT.Silu).then_inc(gT_ready, 1)
                for t in range(TT):
                    act.wait_ge(o_done, TT * hd + t + 1)
                    nc.scalar.copy(otok[0:ROWS[t], t, :], ps[0:ROWS[t], O_BANK[t], :]).then_inc(otok_ready, 1)
                for c in range(2):
                    act.wait_ge(sp_done, 2 * hd + c + 1)
                    nc.scalar.copy(sp_out[:, c, :], ps[:, 6 + c, :]).then_inc(sp_copied, 1)
                for f in range(4):
                    act.wait_ge(ogt_ready, 8 * hd + 2 * f + 2)
                    nc.scalar.copy(ogh[:, f, :], ogt[:, f % 2, :]).then_inc(ogh_ready, 1)
                for s in range(KD):
                    a = 14 + s
                    split_hi(act, u0 + a, q0 + a // 4, a % 4, 4 if a < 20 else KD)
                    if last:
                        act.wait_ge(taken, u0 + 12 + s + 1)
                        x_tile(s, G_FFN2)
                act.wait_ge(sp_stored, 16 * (hd + 1))

            with act.Fori(0, HEADS - 1) as hd:
                head(hd, False)
            head(HEADS - 1, True)
            ffn("ffn2_0", G_KV)

            def take_kv(n0):
                def take(i, s):
                    n = n0 + 4 * i + s
                    if n == 3:
                        act.wait_ge(fwp_ready, 2)
                        nc.scalar.copy(fwh[:, :, :], fwp[:, :, :]).then_inc(fwh_ready, 1)
                    if n == KD - 1:
                        act.wait_ge(gate_step, 3)
                        nc.scalar.activation(le[:, :], la[:, :], ACT.Exp, scale=-1.0).then_inc(exp_ready, 1)
                    if n >= 2:
                        act.wait_ge(kv_stored[s % 2], 32 * (n // 2))
                    act.wait_ge(kvt_done, n + 1)
                    nc.scalar.copy(kvtok[:, s % 2, 0:4, :], ps[:, 4 + 2 * (s % 2), :]
                                   .rearrange("p (i d) -> p i d", i=4)).then_inc(kvtok_ready, 1)
                    nc.scalar.copy(kvtok[0:TS, s % 2, 4, :], ps[0:TS, 5 + 2 * (s % 2), 0:P]).then_inc(kvtok_ready, 1)
                return take
            section(act, "k", split_hi, take_kv(0))
            section(act, "v", split_hi, take_kv(KD))
            act.wait_ge(unit_done, first["ffn1_1_in0"])
            for j in range(KD):
                x_tile(j, G_FFN1 + KD)
            for n in range(2):
                act.wait_ge(kv_stored[n], 32 * KD)
            act.wait_ge(f_stored, 32)
            act.wait_ge(cum_stored, 16)
            ffn("ffn1_1", G_MIX + KD)
            section(act, "q", split_hi, lambda i, s: None)

            def exp_head(t, e):
                act.wait_ge(nmx_ready, 3 * t + e + 1)
                for i in range(4):
                    p = sc[:, e, SOFF[i]:SOFF[i] + KEYS[i]]
                    nc.scalar.activation(p, p, ACT.Exp, bias=nmx[:, e, i:i + 1], accum_out=rsum[:, e, i:i + 1]) \
                        .then_inc(exp_done, 1)

            def exp_sample(t):
                act.wait_ge(nmx_ready, 3 * t + 3)
                nc.scalar.activation(sc_s[:, :], sc_s[:, :], ACT.Exp, bias=nmx[:, 0, 4:5],
                                     accum_out=rsum[:, 0, 4:5]).then_inc(exp_done, 1)

            def cached_keys(t, b):
                act.wait_ge(ckt_done, t + 1)
                nc.scalar.copy(kTc[:, b, :], ps[:, 7, 0:P]).then_inc(kTc_ready, 1)

            def pt_copies(t, e):
                act.wait_ge(pt_done, 8 * t + 3 * e + 1)
                nc.scalar.copy(pt[:, e, 0:512], ps[:, 3, :]).then_inc(pt_act, 1)
                act.wait_ge(pt_done, 8 * t + 3 * e + 3)
                nc.scalar.copy(pt[:, e, 1024:1280], ps[:, 3, 0:256]).then_inc(pt_act, 1)

            def fox_pair(t, b, last=False):
                pt_copies(t, 0)
                exp_head(t, 1)
                exp_sample(t)
                if not last:
                    cached_keys(t + 1, 1 - b)
                pt_copies(t, 1)
                if not last:
                    exp_head(t + 1, 0)
                act.wait_ge(pt_done, 8 * t + 7)
                nc.scalar.copy(pts[:, 0, :], ps[:, 4, 0:P]).then_inc(pt_act, 1)
                act.wait_ge(av_done, 3 * t + 2)
                nc.scalar.copy(xh[:, t, 0:TP], ps[:, 5, :]).then_inc(foxh_ready, 1)
                act.wait_ge(av_done, 3 * t + 3)
                nc.scalar.copy(xh[:, t, TP:T], ps[:, 6, 0:TS]).then_inc(foxh_ready, 1)

            cached_keys(0, 0)
            exp_head(0, 0)
            for b in range(2):
                fox_pair(b, b)
            with act.Fori(1, PAIRS // 2 - 1) as i:
                for b in range(2):
                    fox_pair(2 * i + b, b)
            for b in range(2):
                fox_pair(PAIRS - 2 + b, b, b == 1)

            section(act, "fox_out", split_hi, lambda i, s: None)
            act.wait_ge(taken, first["fox_out"] + KD)
            for j in range(KD):
                x_tile(j, G_FFN2 + KD)
            ffn("ffn2_1", None)
            for t in range(TT):
                act.wait_ge(yt_done, 2 * t + 1)
                nc.scalar.copy(ytok[0:ROWS[t], t, 0:512], ps[0:ROWS[t], 4 + 2 * (t % 2), :]).then_inc(ytok_act, 1)

        @block.vector
        def _(dve):
            n_x, n_norm, n_newton = [0], [0], [0]

            def x_tile(j, gain):
                n_x[0] += 1
                dve.wait_ge(xhi_ready, n_x[0])
                nc.vector.scalar_tensor_tensor(xl[:, j, :], h[:, j, :], gains[:, gain + j:gain + j + 1],
                                               xh[:, j, :].bitcast(F32), ALU.mult, ALU.subtract).then_inc(x_ready, 1)

            def make_rstd():
                n_norm[0] += 1
                dve.wait_ge(msum_ready, n_norm[0])

                def step(instruction):
                    n_newton[0] += 1
                    instruction.then_inc(newton, 1)
                    dve.wait_ge(newton, n_newton[0])
                step(nc.vector.tensor_scalar(halves(sq[:, :]), ps[:, 4:6, 0:HT], 1.0 / D, EPS, ALU.mult, ALU.add))
                step(nc.vector.tensor_scalar(rstd[:, :].bitcast(I32), sq[:, :].bitcast(I32), -0.5, RSQRT_SEED,
                                             ALU.mult, ALU.add))
                for n in range(3):
                    step(nc.vector.tensor_tensor(newt[:, :], rstd[:, :], rstd[:, :], ALU.mult))
                    step(nc.vector.scalar_tensor_tensor(newt[:, :], newt[:, :], -0.5, sq[:, :], ALU.mult, ALU.mult))
                    last = nc.vector.scalar_tensor_tensor(rstd[:, :], newt[:, :], 1.5, rstd[:, :], ALU.add, ALU.mult)
                    if n < 2:
                        step(last)
                last.then_inc(rstd_ready, 1)
                dve.wait_ge(rstd_ready, n_norm[0])

            def take_h(u, s, j, scale, gain):
                dve.wait_ge(unit_done, u + 1)
                nc.vector.scalar_tensor_tensor(halves(h[:, j, :]), unit_psum(s), scale, halves(h[:, j, :]),
                                               ALU.mult, ALU.add).then_inc(taken, 1)
                if gain is not None:
                    x_tile(j, gain)

            pairs = [0]

            def ffn(name, gain, factor=None):
                for part, (j0, n) in enumerate(FF_PARTS):
                    u0, u1, p0 = first[f"{name}_in{part}"], first[f"{name}_out{part}"], pairs[0]

                    def take_in(i, s):
                        b, a = s // 2, p0 + 2 * i + s // 2
                        dve.wait_ge(unit_done, u0 + 4 * i + s + 1)
                        if s % 2 == 0:
                            nc.vector.tensor_tensor(halves(gate[:, b, :]), unit_psum(s), halves(rstd[:, :]), ALU.mult) \
                                .then_inc(taken, 1)
                        else:
                            dve.wait_ge(rsilu_ready, a + 1)
                            nc.vector.tensor_tensor(halves(prod[:, b, :]), unit_psum(s), halves(rsilu[:, b, :]), ALU.mult) \
                                .then_inc(taken, 1)
                            dve.wait_ge(act_hi, a + 1)
                            nc.vector.tensor_tensor(actl[:, 2 * i + b, :], prod[:, b, :],
                                                    acth[:, 2 * i + b, :].bitcast(F32), ALU.subtract).then_inc(act_ready, 1)

                    def take_out(i, s):
                        take_h(u1 + 4 * i + s, s, 4 * i + s, 0.5, gain if part else None)
                    section(dve, f"{name}_in{part}", split_lo, take_in, factor if part == 0 else None)
                    section(dve, f"{name}_out{part}", split_lo, take_out)
                    pairs[0] += n

            nc.vector.memset(ones[:, :], 1.0).then_inc(setup, 1)
            dve.wait_ge(const_in, 16 * 8)
            nc.vector.tensor_copy(idb[:, :], ident).then_inc(setup, 1)
            nc.vector.tensor_copy(trib[:, :], const[:, C_TRI:C_TRI + P]).then_inc(setup, 1)
            nc.vector.tensor_copy(trisb[:, :], const[:, C_TRIS:C_TRIS + TS]).then_inc(setup, 1)
            dve.wait_ge(gains_ready, 1)
            split_lo(dve, 0, 0, 0, KD)
            split_lo(dve, 1, 0, 1, KD)
            for j in range(KD):
                dve.wait_ge(xt_ready, j + 1)
                nc.vector.tensor_copy(h[:, j, 0:TP], ps[:, 4 + 2 * (j % 2), :]).then_inc(h0_ready, 1)
                nc.vector.tensor_copy(h[:, j, TP:T], ps[:, 5 + 2 * (j % 2), 0:TS]).then_inc(h0_ready, 1)
                x_tile(j, G_FFN1)
            ffn("ffn1_0", G_MIX, make_rstd)

            def head(hd, first_head=False, last_head=False):
                u0 = RET + 20 * hd

                def scaled(out, s, factor):
                    nc.vector.scalar_tensor_tensor(halves(out), unit_psum(s), factor, halves(rstd[:, :]),
                                                   ALU.mult, ALU.mult).then_inc(taken, 1)
                for s in range(12):
                    a = s + 2
                    split_lo(dve, u0 + a, None, a % 4, KD if a < 12 else 4)
                    if first_head and s == 0:
                        make_rstd()
                    dve.wait_ge(unit_done, u0 + s + 1)
                    if s < 4:
                        a = s // 2
                        if s == 2:
                            dve.wait_ge(rope_pmul, 4 * hd + 2)
                        scaled(rt[:, s % 2, :], s, DK ** -0.5 if a == 0 else 1.0)
                        if s % 2:
                            dve.wait_ge(taken, u0 + s + 1)
                            nc.vector.tensor_tensor(rt[:, 2, :], rt[:, 0, :], const[:, C_COS:C_COS + T], ALU.mult) \
                                .then_inc(rope_mul, 1)
                            nc.vector.tensor_tensor(rt[:, 3, :], rt[:, 1, :], const[:, C_SIN:C_SIN + T], ALU.mult) \
                                .then_inc(rope_mul, 1)
                            dve.wait_ge(rope_mul, 4 * hd + 2 * a + 2)
                            nc.vector.tensor_tensor(qk[:, 2 * a, :], rt[:, 2, :], rt[:, 3, :], ALU.subtract) \
                                .then_inc(rope_dve, 1)
                    elif s < 8:
                        scaled(vT[:, s - 4, :], s, 1.0)
                    else:
                        scaled(gT[:, s - 8, :], s, 1.0)
                for t in range(TT):
                    dve.wait_ge(kt_done, TT * hd + t + 1)
                    nc.vector.tensor_scalar(ktok[0:ROWS[t], t, :], ps[0:ROWS[t], 6 + t % 2, 0:DK],
                                            const[0:ROWS[t], bass.ds(C_KDEC + TT * hd + t, 1)], None, ALU.mult) \
                        .then_inc(ktok_ready, 1)
                dve.wait_ge(head_in, 32 * (hd + 1))
                for t in range(4):
                    dve.wait_ge(s_done, TT * hd + t + 1)
                    w = TP - P * t
                    nc.vector.tensor_tensor(sT[:, STOFF[t]:STOFF[t] + w], ps[:, 4 + t, 0:w], dm[:, 0:w], ALU.mult) \
                        .then_inc(sT_ready, 1)
                dve.wait_ge(s_done, TT * hd + 5)
                nc.vector.tensor_tensor(sT[0:TS, 1280:1280 + TS], ps[0:TS, 4, 0:TS], dm[0:TS, 0:TS], ALU.mult) \
                    .then_inc(sT_ready, 1)

                g0, n = GN_STEPS * hd, 0
                for t in range(TT):
                    dve.wait_ge(otok_ready, TT * hd + t + 1)
                    nc.vector.bn_stats(bst[0:ROWS[t], t, :], otok[0:ROWS[t], t, :]).then_inc(gn_step, 1)
                dve.wait_ge(gn_step, g0 + TT)
                nc.vector.memset(scrap[:, :], 0.0).then_inc(gn_step, 1)
                for t in range(TT):
                    nc.vector.bn_aggr(mv[0:ROWS[t], t, :], bst[0:ROWS[t], t, :]).then_inc(gn_step, 1)
                n = 2 * TT + 1
                dve.wait_ge(gn_step, g0 + n)

                def step(instruction):
                    nonlocal n
                    n += 1
                    instruction.then_inc(gn_step, 1)
                    dve.wait_ge(gn_step, g0 + n)
                step(nc.vector.tensor_scalar(gx[:, :], mv[:, :, 1], 1.0, EPS, ALU.mult, ALU.add))
                step(nc.vector.tensor_scalar(gy[:, :].bitcast(I32), gx[:, :].bitcast(I32), -0.5, RSQRT_SEED,
                                             ALU.mult, ALU.add))
                for _ in range(3):
                    step(nc.vector.tensor_tensor(ga[:, :], gy[:, :], gy[:, :], ALU.mult))
                    step(nc.vector.scalar_tensor_tensor(ga[:, :], ga[:, :], -0.5, gx[:, :], ALU.mult, ALU.mult))
                    step(nc.vector.scalar_tensor_tensor(gy[:, :], ga[:, :], 1.5, gy[:, :], ALU.add, ALU.mult))
                assert n == GN_STEPS
                for t in range(TT):
                    o = otok[0:ROWS[t], t, :]
                    nc.vector.tensor_scalar(o, o, mv[0:ROWS[t], t, 0:1], gy[0:ROWS[t], t:t + 1],
                                            ALU.subtract, ALU.mult).then_inc(on_ready, 1)
                for c in range(2):
                    dve.wait_ge(sn_done, 2 * hd + c + 1)
                    nc.vector.scalar_tensor_tensor(s0[:, c, :], s0[:, c, :], const[:, bass.ds(C_GCH + hd, 1)],
                                                   ps[:, 4 + c, :], ALU.mult, ALU.add).then_inc(sn_ready, 1)
                dve.wait_ge(rope_pmul, 4 * hd + 4)
                for f in range(4):
                    gn = gains[:, bass.ds(G_GN + 4 * hd + f, 1)]
                    dve.wait_ge(ot_done, 4 * hd + f + 1)
                    dve.wait_ge(gT_ready, 4 * hd + f + 1)
                    nc.vector.scalar_tensor_tensor(ogt[:, f % 2, 0:TP], ps[:, 6 + f % 2, :], gn, gT[:, f, 0:TP],
                                                   ALU.mult, ALU.mult).then_inc(ogt_ready, 1)
                    nc.vector.scalar_tensor_tensor(ogt[:, f % 2, TP:T], ps[:, 4 + f % 2, 0:TS], gn, gT[:, f, TP:T],
                                                   ALU.mult, ALU.mult).then_inc(ogt_ready, 1)
                    dve.wait_ge(ogh_ready, 4 * hd + f + 1)
                    nc.vector.tensor_tensor(ogl[:, f, :], ogt[:, f % 2, :], ogh[:, f, :].bitcast(F32), ALU.subtract) \
                        .then_inc(og_ready, 1)
                for s in range(KD):
                    a = 14 + s
                    split_lo(dve, u0 + a, None, a % 4, 4 if a < 20 else KD)
                    take_h(u0 + 12 + s, s, s, 1.0, G_FFN2 if last_head else None)

            nc.vector.memset(mv[:, :, :], 1.0).then_inc(setup, 1)
            head(0, first_head=True)
            with dve.Fori(1, HEADS - 1) as hd:
                head(hd)
            head(HEADS - 1, last_head=True)
            ffn("ffn2_0", G_KV, make_rstd)

            nc.vector.memset(fwp[:, :, :], 0.0).then_inc(fwp_ready, 1)

            n_gate = [0]

            def step(instruction):
                n_gate[0] += 1
                instruction.then_inc(gate_step, 1)
                dve.wait_ge(gate_step, n_gate[0])

            def log_gates():
                dve.wait_ge(f_done, 1)
                step(nc.vector.tensor_tensor(halves(lz[:, :]), ps[0:FOX_HEADS, 4:6, 0:HT], halves(rstd[0:FOX_HEADS, :]),
                                             ALU.mult))
                step(nc.vector.tensor_scalar(lz[:, :], lz[:, :], bf[:, 0:1], None, ALU.add))
                step(nc.vector.scalar_tensor_tensor(la[:, :], lz[:, :], -1.0, lz[:, :], ALU.mult, ALU.max))
                step(nc.vector.tensor_scalar(lm[:, :], lz[:, :], 0.0, None, ALU.min))
                dve.wait_ge(exp_ready, 1)
                step(nc.vector.tensor_scalar(lp[:, :], le[:, :], 2.0, None, ALU.add))
                step(nc.vector.reciprocal(lp[:, :], lp[:, :]))
                step(nc.vector.tensor_tensor(ls[:, :], le[:, :], lp[:, :], ALU.mult))
                step(nc.vector.tensor_tensor(la[:, :], ls[:, :], ls[:, :], ALU.mult))
                step(nc.vector.tensor_scalar(lp[:, :], la[:, :], 1.0 / 15, None, ALU.mult))
                for d in (13, 11, 9, 7, 5, 3):
                    step(nc.vector.scalar_tensor_tensor(lp[:, :], lp[:, :], 1.0 / d, la[:, :], ALU.add, ALU.mult))
                step(nc.vector.scalar_tensor_tensor(lp[:, :], lp[:, :], 1.0, ls[:, :], ALU.add, ALU.mult))
                nc.vector.scalar_tensor_tensor(logf[:, :], lp[:, :], -2.0, lm[:, :], ALU.mult, ALU.add).then_inc(logf_ready, 1)
                dve.wait_ge(logf_ready, 1)

            def sum_gates():
                dve.wait_ge(ft_done, 1)
                nc.vector.tensor_copy(ftok[:, 0:4, :], ps[:, 6, 0:4 * FOX_HEADS].rearrange("p (i h) -> p i h", i=4)) \
                    .then_inc(ftok_ready, 1)
                nc.vector.tensor_copy(ftok[0:TS, 4, :], ps[0:TS, 6, 64:64 + FOX_HEADS]).then_inc(ftok_ready, 1)
                step(nc.vector.tensor_copy(catf[:, 0:PAST], ps[0:FOX_HEADS, 6, 128:128 + PAST]))
                step(nc.vector.tensor_copy(catf[:, PAST:], logf[:, TP:T]))
                step(nc.vector.memset(ones_row[:, :], 1.0))
                step(nc.vector.tensor_tensor_scan(cumf[:, 0:TP], ones_row[:, :], logf[:, 0:TP], 0.0, ALU.mult, ALU.add))
                step(nc.vector.tensor_tensor_scan(cumf[:, TP:], ones_row[:, 0:PAST + TS], catf[:, :], 0.0, ALU.mult, ALU.add))
                nc.vector.tensor_scalar(cumf[:, :], cumf[:, :], -1.0, None, ALU.mult).then_inc(cum_ready, 1)

            def take_kv(u0, n0):
                def take(i, s):
                    n = n0 + 4 * i + s
                    if n == 2:
                        dve.wait_ge(fwp_ready, 1)
                        dve.wait_ge(fw_in, 32)
                        nc.vector.tensor_copy(fwp[:, :, 0:FOX_HEADS], fw[:, :, :]).then_inc(fwp_ready, 1)
                    if n == 5:
                        dve.wait_ge(fwh_ready, 1)
                        nc.vector.tensor_tensor(fwl[:, :, :], fwp[:, :, :], fwh[:, :, :].bitcast(F32), ALU.subtract) \
                            .then_inc(fw_ready, 1)
                    if n == KD + 1:
                        sum_gates()
                    dve.wait_ge(unit_done, u0 + 4 * i + s + 1)
                    if n >= 2:
                        dve.wait_ge(kvt_done, n - 1)
                        dve.wait_ge(kT_stored[s % 2], 16 * min(n // 2, KD // 2))
                    nc.vector.tensor_tensor(halves(kvt[:, s % 2, :]), unit_psum(s), halves(rstd[:, :]), ALU.mult) \
                        .then_inc(taken, 1)
                return take
            section(dve, "k", split_lo, take_kv(first["k"], 0), make_rstd)
            log_gates()
            section(dve, "v", split_lo, take_kv(first["v"], KD))
            for j in range(KD):
                x_tile(j, G_FFN1 + KD)

            for n in range(2):
                dve.wait_ge(kv_stored[n], 32 * KD)
            dve.wait_ge(f_stored, 32)
            dve.wait_ge(cum_stored, 16)
            ffn("ffn1_1", G_MIX + KD)

            def take_q(i, s):
                dve.wait_ge(unit_done, first["q"] + 4 * i + s + 1)
                nc.vector.scalar_tensor_tensor(halves(qT[:, 4 * i + s, :]), unit_psum(s), (D // FOX_HEADS) ** -0.5,
                                               halves(rstd[:, :]), ALU.mult, ALU.mult).then_inc(taken, 1)
            section(dve, "q", split_lo, take_q, make_rstd)

            def biased(out, scores, b, top):
                nc.vector.tensor_tensor_reduce(out=out, in0=scores, in1=b, scale=1.0, scalar=LEAST, op0=ALU.add,
                                               op1=ALU.max, accum_out=top).then_inc(max_ready, 1)

            def max_head(t, b, e):
                if not (isinstance(t, int) and 3 * t + e == 0):
                    dve.wait_ge(scrapped, 3 * t + e)
                dve.wait_ge(qk_done, 3 * t + e + 1)
                nc.vector.memset(scrap[:, :], 0.0).then_inc(scrapped, 1)
                for i in range(4):
                    bank, c0 = S_BANK[i]
                    biased(sc[:, e, SOFF[i]:SOFF[i] + KEYS[i]], ps[:, bank, c0:c0 + KEYS[i]],
                           bias[:, b, e, 0:KEYS[i]], mx[:, e, i:i + 1])
                dve.wait_ge(max_ready, 9 * t + 4 * e + 4)
                nc.vector.tensor_scalar(nmx[:, e, 0:4], mx[:, e, 0:4], -1.0, None, ALU.mult).then_inc(nmx_ready, 1)

            def max_sample(t, b):
                dve.wait_ge(scrapped, 3 * t + 2)
                dve.wait_ge(qk_done, 3 * t + 3)
                nc.vector.memset(scrap[:, :], 0.0).then_inc(scrapped, 1)
                biased(sc_s[:, :], ps[:, 7, 0:PAST + TS], bias_s[:, b, :], mx[:, 0, 4:5])
                dve.wait_ge(max_ready, 9 * t + 9)
                nc.vector.tensor_scalar(nmx[:, 0, 4:5], mx[:, 0, 4:5], -1.0, None, ALU.mult).then_inc(nmx_ready, 1)

            def normalise_head(t, e):
                dve.wait_ge(exp_done, 9 * t + 4 * e + 4)
                nc.vector.reciprocal(rinv[:, e, 0:4], rsum[:, e, 0:4]).then_inc(rinv_ready, 1)
                dve.wait_ge(rinv_ready, 3 * t + e + 1)
                for i in range(4):
                    p = sc[:, e, SOFF[i]:SOFF[i] + KEYS[i]]
                    nc.vector.tensor_scalar(p, p, rinv[:, e, i:i + 1], None, ALU.mult).then_inc(p_ready, 1)

            def normalise_sample(t):
                dve.wait_ge(exp_done, 9 * t + 9)
                nc.vector.reciprocal(rinv[:, 0, 4:5], rsum[:, 0, 4:5]).then_inc(rinv_ready, 1)
                dve.wait_ge(rinv_ready, 3 * t + 3)
                nc.vector.tensor_scalar(sc_s[:, :], sc_s[:, :], rinv[:, 0, 4:5], None, ALU.mult).then_inc(p_ready, 1)

            def pt_copy(t, e):
                dve.wait_ge(pt_done, 8 * t + 3 * e + 2)
                nc.vector.tensor_copy(pt[:, e, 512:1024], ps[:, 4, :]).then_inc(pt_dve, 1)

            def fox_pair(t, b, last=False):
                normalise_head(t, 0)
                max_head(t, b, 1)
                pt_copy(t, 0)
                max_sample(t, b)
                normalise_head(t, 1)
                normalise_sample(t)
                if not last:
                    dve.wait_ge(pt_done, 8 * t + 3)
                    max_head(t + 1, 1 - b, 0)
                pt_copy(t, 1)
                dve.wait_ge(pt_done, 8 * t + 8)
                nc.vector.tensor_copy(pts[0:TS, 1, :], ps[0:TS, 3, 0:P]).then_inc(pt_dve, 1)
                for n, (a, z, bank) in enumerate(((0, TP, 5), (TP, T, 6))):
                    dve.wait_ge(foxh_ready, 2 * t + n + 1)
                    nc.vector.tensor_tensor(xl[:, t, a:z], ps[:, bank, 0:z - a], xh[:, t, a:z].bitcast(F32), ALU.subtract) \
                        .then_inc(fox_ready, 1)

            dve.wait_ge(pair_in[0], 16 * PAIR_LOADS)
            max_head(0, 0, 0)
            for b in range(2):
                fox_pair(b, b)
            with dve.Fori(1, PAIRS // 2 - 1) as i:
                for b in range(2):
                    fox_pair(2 * i + b, b)
            for b in range(2):
                fox_pair(PAIRS - 2 + b, b, b == 1)

            def take_fox(i, s):
                take_h(first["fox_out"] + 4 * i + s, s, 4 * i + s, 1.0, None)
            section(dve, "fox_out", split_lo, take_fox)
            for j in range(KD):
                x_tile(j, G_FFN2 + KD)
            ffn("ffn2_1", None, make_rstd)
            make_rstd()
            for j in range(KD):
                nc.vector.scalar_tensor_tensor(yT[:, j, :], h[:, j, :], gains[:, G_FIN + j:G_FIN + j + 1], rstd[:, :],
                                               ALU.mult, ALU.mult).then_inc(y_ready, 1)
            for t in range(TT):
                dve.wait_ge(yt_done, 2 * t + 2)
                nc.vector.tensor_copy(ytok[0:ROWS[t], t, 512:], ps[0:ROWS[t], 5 + 2 * (t % 2), :]).then_inc(ytok_dve, 1)

        @block.gpsimd
        def _(pool):
            n_sq, n_norm, n_pair = [0], [0], [0]

            def sum_squares(ready):
                if n_norm[0]:
                    pool.wait_ge(msum_ready, n_norm[0])
                for j in range(KD):
                    ready(j)
                    out = sq if j else ssq
                    nc.gpsimd.tensor_tensor(out[:, :], h[:, j, :], h[:, j, :], ALU.mult).then_inc(sq_step, 1)
                    n_sq[0] += 1
                    pool.wait_ge(sq_step, n_sq[0])
                    if j:
                        add = nc.gpsimd.tensor_tensor(ssq[:, :], ssq[:, :], sq[:, :], ALU.add)
                        if j < KD - 1:
                            add.then_inc(sq_step, 1)
                            n_sq[0] += 1
                            pool.wait_ge(sq_step, n_sq[0])
                        else:
                            add.then_inc(ssq_ready, 1)
                            n_norm[0] += 1

            def h_taken(u0):
                return lambda j: pool.wait_ge(taken, u0 + j + 1)

            def ffn(name):
                for part, (j0, n) in enumerate(FF_PARTS):
                    p0 = n_pair[0]
                    pool.wait_ge(rstd_ready, n_norm[0])
                    with pool.Fori(0, n // 2) as i:
                        for b in range(2):
                            pool.wait_ge(silu_ready, p0 + 2 * i + b + 1)
                            nc.gpsimd.tensor_tensor(rsilu[:, b, :], silu[:, b, :], rstd[:, :], ALU.mult) \
                                .then_inc(rsilu_ready, 1)
                    n_pair[0] += n
                sum_squares(h_taken(first[f"{name}_out1"]))

            sum_squares(lambda j: pool.wait_ge(h0_ready, 2 * j + 2))
            ffn("ffn1_0")

            state = A["state_ret"][0, 0].rearrange("h (c p) e -> h p c e", p=P)
            state_p = O["state_ret_prompt"][0, 0].rearrange("h (c p) e -> h p c e", p=P)
            state_s = O["state_ret_sample"][0, 0].rearrange("h (c p) e -> h p c e", p=P)

            def head_loads(hd):
                pool.dma_start(dm[:, :], A["decay_mask"][hd]).then_inc(head_in, 16)
                pool.dma_start(s0[:, :, :], state[hd]).then_inc(head_in, 16)

            def head(hd, last=False):
                for a in range(2):
                    pool.wait_ge(taken, RET + 20 * hd + 2 * a + 2)
                    nc.gpsimd.tensor_tensor(rt[:, 4, :], rt[:, 0, :], const[:, C_SIN:C_SIN + T], ALU.mult) \
                        .then_inc(rope_pmul, 1)
                    nc.gpsimd.tensor_tensor(rt[:, 5, :], rt[:, 1, :], const[:, C_COS:C_COS + T], ALU.mult) \
                        .then_inc(rope_pmul, 1)
                    pool.wait_ge(rope_pmul, 4 * hd + 2 * a + 2)
                    nc.gpsimd.tensor_tensor(qk[:, 2 * a + 1, :], rt[:, 4, :], rt[:, 5, :], ALU.add).then_inc(rope_pool, 1)
                    pool.wait_ge(rope_pool, 2 * hd + a + 1)
                pool.wait_ge(rope_dve, 2 * hd + 1)
                for c in range(2):
                    nc.gpsimd.tensor_tensor(qd[:, c, :], qk[:, c, TP:T], const[:, bass.ds(C_QDEC + TS * hd, TS)], ALU.mult) \
                        .then_inc(qd_ready, 1)
                apart(pool)
                pool.wait_ge(sp_copied, 2 * hd + 2)
                pool.dma_start(state_p[hd], sp_out[:, :, :]).then_inc(sp_stored, 16)
                apart(pool)
                pool.wait_ge(sn_ready, 2 * hd + 2)
                pool.dma_start(state_s[hd], s0[:, :, :]).then_inc(sn_stored, 16)
                if not last:
                    apart(pool)
                    pool.wait_ge(sn_stored, 16 * (hd + 1))
                    head_loads(hd + 1)

            pool.wait_ge(unit_done, RET)
            head_loads(0)
            with pool.Fori(0, HEADS - 1) as hd:
                head(hd)
            head(HEADS - 1, True)
            sum_squares(h_taken(RET + 20 * (HEADS - 1) + 12))
            ffn("ffn2_0")

            pool.wait_ge(unit_done, first["k"])
            pool.dma_start(fw[:, :, :], A["fox_w_kvf"][:, 2 * D:].rearrange("(k p) h -> p k h", p=P)).then_inc(fw_in, 16)
            pool.dma_start(clf[:, :], A["cache_logf"][0]).then_inc(fw_in, 16)
            keys_out = kT_dram.rearrange("(t p) n -> t p n", p=P)
            for name, n0 in (("k", 0), ("v", KD)):
                out_p = O[f"{name}_prompt"][0].rearrange("(i p) (t e) d -> t p i (e d)", p=P, e=2)
                out_s = O[f"{name}_sample"][0].rearrange("n (t e) d -> t n (e d)", e=2)
                with pool.Fori(0, KD // 2) as i:
                    for b in range(2):
                        t = 2 * i + b
                        if name == "k":
                            apart(pool)
                            pool.wait_ge(taken, first["k"] + t + 1)
                            pool.dma_start(keys_out[t], kvt[:, b, :]).then_inc(kT_stored[b], 16)
                        apart(pool)
                        pool.wait_ge(kvtok_ready, 2 * (n0 + t) + 2)
                        pool.dma_start(out_p[t], kvtok[:, b, 0:4, :]).then_inc(kv_stored[b], 16)
                        pool.dma_start(out_s[t], kvtok[0:TS, b, 4, :]).then_inc(kv_stored[b], 16)
            pool.wait_ge(ftok_ready, 2)
            pool.dma_start(O["logf_prompt"][0].rearrange("(i p) h -> p i h", p=P), ftok[:, 0:4, :]).then_inc(f_stored, 16)
            pool.dma_start(O["logf_sample"][0], ftok[0:TS, 4, :]).then_inc(f_stored, 16)
            pool.wait_ge(cum_ready, 1)
            pool.dma_start(cum_dram, cumf[:, :]).then_inc(cum_stored, 16)
            ffn("ffn1_1")

            pool.wait_ge(unit_done, first["q"])
            nc.gpsimd.memset(qpad[:, :, :, :], 0.0).then_inc(pad_zero, 1)
            nc.gpsimd.memset(qpad_s[:, :, :], 0.0).then_inc(pad_zero, 1)
            pool.wait_ge(pad_zero, 2)

            def pad(t, b):
                for e in range(2):
                    r = slice(TS * e, TS * e + TS)
                    nc.gpsimd.tensor_copy(qpad[r, b, e, :], qT[r, t, 0:TP]).then_inc(qpad_ready, 1)
                    nc.gpsimd.tensor_copy(qpad_s[r, b, TS * e:TS * e + TS], qT[r, t, TP:T]).then_inc(qpad_ready, 1)
            pool.wait_ge(taken, first["q"] + 1)
            pad(0, 0)
            pool.wait_ge(taken, first["q"] + 2)
            pad(1, 1)
            with pool.Fori(1, PAIRS // 2) as i:
                for b in range(2):
                    pool.wait_ge(taken, first["q"] + 2 * i + b + 1)
                    pool.wait_ge(qk_done, 3 * (2 * i + b - 1))
                    pad(2 * i + b, b)
            sum_squares(h_taken(first["fox_out"]))
            ffn("ffn2_1")

            for t in range(TT):
                pool.wait_ge(ytok_act, t + 1)
                pool.wait_ge(ytok_dve, t + 1)
                out = O["y_prompt"][0, P * t:P * t + P, :] if t < 4 else O["y_sample"][0]
                pool.dma_start(out, ytok[0:ROWS[t], t, :]).then_inc(y_stored, 16)
            pool.wait_ge(y_stored, 16 * TT)
            pool.wait_ge(sp_stored, 16 * HEADS)
            pool.wait_ge(sn_stored, 16 * HEADS)
            for n in range(2):
                pool.wait_ge(kv_stored[n], 32 * KD)
            pool.wait_ge(f_stored, 32)

        @block.tensor
        def _(pe):
            def product(out, terms, start, stop):
                for n, (w, x) in enumerate(terms):
                    for a in range(2):
                        mm = nc.tensor.matmul(out[:, a, :], w, x[:, a * HT:(a + 1) * HT],
                                              start=start and n == 0, stop=stop and n == len(terms) - 1)
                return mm

            def unit(u, s, kt, mh, ml, before_block=None):
                pe.wait_ge(lo_ready, u + 1)
                if not (isinstance(u, int) and u < 2):
                    pe.wait_ge(taken, u - 1)
                for k in range(kt):
                    if before_block is not None:
                        before_block(k)
                    b = s % SPLIT
                    mm = product(unit_psum(s), ((wl[:, b, k, :], mh[:, k, :]), (wh[:, b, k, :], ml[:, k, :]),
                                                (wh[:, b, k, :], mh[:, k, :])), k == 0, k == kt - 1)
                mm.then_inc(unit_done, 1)

            n_x, n_norm, n_act = [0], [0], [0]

            def x_arrives():
                n0 = n_x[0]
                n_x[0] += KD
                return lambda k: pe.wait_ge(x_ready, n0 + k + 1)

            def sum_partitions():
                n_norm[0] += 1
                pe.wait_ge(ssq_ready, n_norm[0])
                for a in range(2):
                    mm = nc.tensor.matmul(ps[:, 4 + a, 0:HT], ones[:, :], ssq[:, a * HT:(a + 1) * HT], start=True, stop=True)
                mm.then_inc(msum_ready, 1)

            def units(name, mh, ml, arrives=None, norm=False):
                u0, n4, kt = first[name], units_of[name] // 4, blocks[name]

                def four(i, waits=None):
                    for s in range(4):
                        unit(u0 + 4 * i + s, s, kt, mh, ml, waits if s == 0 else None)
                        if waits is not None and norm and s == 0:
                            sum_partitions()
                four(0, arrives or (lambda k: None))
                with pe.Fori(1, n4) as i:
                    four(i)

            def ffn(name, norm=True):
                for part, (j0, n) in enumerate(FF_PARTS):
                    units(f"{name}_in{part}", xh, xl, x_arrives() if part == 0 else None, norm and part == 0)
                    n0 = n_act[0]
                    n_act[0] += n
                    units(f"{name}_out{part}", acth, actl, lambda k: pe.wait_ge(act_ready, n0 + k + 1))

            pe.wait_ge(const_in, 16 * 8)
            nc.tensor.transpose(ps[:, 3, 0:G_ALL], grow[:, :], ident[0:G_ALL, 0:G_ALL]).then_inc(gt_ready, 1)
            pe.wait_ge(x_in, 32)
            for j in range(KD):
                if j >= 2:
                    pe.wait_ge(h0_ready, 2 * (j - 1))
                for t in range(TT):
                    r = ROWS[t]
                    out = ps[:, 4 + 2 * (j % 2), P * t:P * t + P] if t < 4 else ps[:, 5 + 2 * (j % 2), 0:TS]
                    mm = nc.tensor.transpose(out, xtok[0:r, t, P * j:P * j + P], ident[0:r, 0:r])
                mm.then_inc(xt_ready, 1)
            pe.wait_ge(gains_ready, 1)
            pe.wait_ge(setup, 4)
            ffn("ffn1_0")

            def head(hd, first_head=False):
                u0 = RET + 20 * hd
                for s in range(12):
                    unit(u0 + s, s, KD, xh, xl, x_arrives() if first_head and s == 0 else None)
                    if first_head and s == 0:
                        sum_partitions()
                pe.wait_ge(taken, u0 + 8)
                pe.wait_ge(rope_dve, 2 * hd + 2)
                pe.wait_ge(rope_pool, 2 * hd + 2)
                for t in range(TT):
                    r = ROWS[t]
                    if 2 <= t < 4:
                        pe.wait_ge(vtok_ready, TT * hd + t - 1)
                        pe.wait_ge(ktok_ready, TT * hd + t - 1)
                    for f in range(4):
                        mm = nc.tensor.transpose(ps[0:r, 4 + t % 2, P * f:P * f + P], vT[:, f, P * t:P * t + r], ident)
                    mm.then_inc(vt_done, 1)
                    for c in range(2):
                        if (t, c) == (3, 1):
                            pe.wait_ge(vtok_ready, TT * hd + 3)
                            pe.wait_ge(ktok_ready, TT * hd + 3)
                        mm = nc.tensor.transpose(ps[0:r, 6 + t % 2, P * c:P * c + P], qk[:, 2 + c, P * t:P * t + r], ident)
                    mm.then_inc(kt_done, 1)
                pe.wait_ge(vtok_ready, TT * hd + TT)
                pe.wait_ge(ktok_ready, TT * hd + TT)
                for t in range(4):
                    for c in range(2):
                        mm = nc.tensor.matmul(ps[:, 4 + t, 0:TP - P * t], qk[:, 2 + c, P * t:P * t + P], qk[:, c, P * t:TP],
                                              start=c == 0, stop=c == 1)
                    mm.then_inc(s_done, 1)
                pe.wait_ge(sT_ready, TT * hd + 1)
                for c in range(2):
                    mm = nc.tensor.matmul(ps[0:TS, 4, 0:TS], qk[:, 2 + c, TP:T], qk[:, c, TP:T], start=c == 0, stop=c == 1)
                mm.then_inc(s_done, 1)
                for i in range(4):
                    pe.wait_ge(sT_ready, TT * hd + i + 2)
                    for t in range(i + 1):
                        c0 = STOFF[t] + P * (i - t)
                        mm = nc.tensor.matmul(ps[:, O_BANK[i], :], sT[:, c0:c0 + P], vtok[:, t, :], start=t == 0, stop=t == i)
                    mm.then_inc(o_done, 1)
                pe.wait_ge(otok_ready, TT * hd + 1)
                pe.wait_ge(qd_ready, 2 * hd + 2)
                pe.wait_ge(head_in, 32 * (hd + 1))
                for c in range(2):
                    nc.tensor.matmul(ps[0:TS, O_BANK[4], :], qd[:, c, :], s0[:, c, :], start=c == 0, stop=False)
                nc.tensor.matmul(ps[0:TS, O_BANK[4], :], sT[0:TS, 1280:1280 + TS], vtok[0:TS, 4, :], start=False, stop=True) \
                    .then_inc(o_done, 1)
                for c in range(2):
                    pe.wait_ge(otok_ready, TT * hd + 2 + c)
                    for t in range(4):
                        mm = nc.tensor.matmul(ps[:, 6 + c, :], ktok[:, t, P * c:P * c + P], vtok[:, t, :], start=t == 0, stop=t == 3)
                    mm.then_inc(sp_done, 1)
                for c in range(2):
                    pe.wait_ge(otok_ready, TT * hd + 4 + c)
                    nc.tensor.matmul(ps[:, 4 + c, :], ktok[0:TS, 4, P * c:P * c + P], vtok[0:TS, 4, :], start=True, stop=True) \
                        .then_inc(sn_done, 1)
                pe.wait_ge(on_ready, TT * hd + TT)
                for f in range(4):
                    if f < 2:
                        pe.wait_ge(sp_copied, 2 * hd + f + 1)
                        pe.wait_ge(sn_ready, 2 * hd + f + 1)
                    else:
                        pe.wait_ge(ogt_ready, 8 * hd + 2 * (f - 1))
                    for t in range(TT):
                        r = ROWS[t]
                        out = ps[:, 6 + f % 2, P * t:P * t + P] if t < 4 else ps[:, 4 + f % 2, 0:TS]
                        mm = nc.tensor.transpose(out, otok[0:r, t, P * f:P * f + P], ident[0:r, 0:r])
                    mm.then_inc(ot_done, 1)
                for s in range(KD):
                    unit(u0 + 12 + s, s, 4, ogh, ogl,
                         (lambda k: pe.wait_ge(og_ready, 4 * hd + k + 1)) if s == 0 else None)

            head(0, True)
            with pe.Fori(1, HEADS) as hd:
                head(hd)
            ffn("ffn2_0")

            def by_token(n, s):
                pe.wait_ge(taken, first["k"] + n + 1)
                if not (isinstance(n, int) and n < 2):
                    pe.wait_ge(kvtok_ready, 2 * (n - 1))
                for t in range(TT):
                    r = ROWS[t]
                    out = ps[:, 4 + 2 * (s % 2), P * t:P * t + P] if t < 4 else ps[0:TS, 5 + 2 * (s % 2), 0:P]
                    mm = nc.tensor.transpose(out, kvt[:, s % 2, P * t:P * t + r], ident)
                mm.then_inc(kvt_done, 1)
            u0 = first["k"]
            for s in range(4):
                unit(u0 + s, s, KD, xh, xl, x_arrives() if s == 0 else None)
                if s == 0:
                    sum_partitions()
                else:
                    by_token(s - 1, s - 1)
            for s in range(4):
                unit(u0 + 4 + s, s, KD, xh, xl)
                by_token(3 + s, (s - 1) % 4)
            pe.wait_ge(kvtok_ready, 2 * (KD - 1))
            pe.wait_ge(fw_ready, 1)
            for k in range(KD):
                mm = product(ps[:, 4:6, 0:HT], ((fwl[:, k, :], xh[:, k, :]), (fwh[:, k, :], xl[:, k, :]),
                                                (fwh[:, k, :], xh[:, k, :])), k == 0, k == KD - 1)
            mm.then_inc(f_done, 1)
            for s in range(4):
                unit(u0 + KD + s, s, KD, xh, xl)
                if s == 1:
                    pe.wait_ge(logf_ready, 1)
                    pe.wait_ge(fw_in, 32)
                    pe.wait_ge(kvtok_ready, 2 * KD)
                    for t in range(TT):
                        r = ROWS[t]
                        nc.tensor.transpose(ps[0:r, 6, FOX_HEADS * t:FOX_HEADS * (t + 1)], logf[:, P * t:P * t + r],
                                            ident[0:FOX_HEADS, 0:FOX_HEADS])
                    nc.tensor.transpose(ps[0:FOX_HEADS, 6, 128:256], clf[:, :], ident).then_inc(ft_done, 1)
                by_token(KD + s - 1, (s - 1) % 4)
            for s in range(4):
                unit(u0 + KD + 4 + s, s, KD, xh, xl)
                by_token(KD + 3 + s, (s - 1) % 4)
            by_token(2 * KD - 1, 3)

            ffn("ffn1_1", norm=False)
            units("q", xh, xl, x_arrives(), True)

            def scores_head(t, b, e):
                pe.wait_ge(qpad_ready, 4 * t + 4)
                for i in (0, 2, 1, 3):
                    bank, c0 = S_BANK[i]
                    out = ps[:, bank, c0:c0 + KEYS[i]]
                    nc.tensor.matmul(out, qpad[:, b, e, P * i:P * i + P], kTp[:, b, 0:KEYS[i]], start=True, stop=False)
                    mm = nc.tensor.matmul(out[:, KEYS[i] - P:], idb[:, :], trib[:, :], start=False, stop=True)
                mm.then_inc(qk_done, 1)

            def cached_keys(t, b, rounds):
                pe.wait_ge(pair_in[b], 16 * PAIR_LOADS * rounds)
                nc.tensor.transpose(ps[:, 7, 0:P], ckp[:, b, :], ident).then_inc(ckt_done, 1)

            def scores_sample(t, b):
                pe.wait_ge(kTc_ready, t + 1)
                nc.tensor.matmul(ps[:, 7, 0:PAST], qpad_s[:, b, :], kTc[:, b, :], start=True, stop=True)
                nc.tensor.matmul(ps[:, 7, PAST:PAST + TS], qpad_s[:, b, :], kTp[:, b, TP:T], start=True, stop=False)
                nc.tensor.matmul(ps[:, 7, PAST:PAST + TS], idb[:, :], trisb[:, :], start=False, stop=True).then_inc(qk_done, 1)

            def values_head(t, b, e, start):
                def turn(i, j, bank):
                    c0 = (PTOFF[j] + P * (i - j)) % 512
                    return nc.tensor.transpose(ps[:, bank, c0:c0 + P], sc[:, e, SOFF[i] + P * j:SOFF[i] + P * j + P], ident)
                pe.wait_ge(p_ready, 9 * t + 4 * e + 4)
                if not start or e:
                    pe.wait_ge(pt_act, 5 * t + 2 * e)
                    pe.wait_ge(pt_dve, 3 * t + e)
                for i in range(4):
                    mm = turn(i, 0, 3)
                mm.then_inc(pt_done, 1)
                for i, j in ((1, 1), (2, 1), (3, 1), (3, 3)):
                    mm = turn(i, j, 4)
                mm.then_inc(pt_done, 1)
                pe.wait_ge(pt_act, 5 * t + 2 * e + 1)
                for i in (2, 3):
                    mm = turn(i, 2, 3)
                mm.then_inc(pt_done, 1)
                out = ps[TS * e:TS * e + TS, 5, :]
                if not start:
                    pe.wait_ge(fox_ready, 2 * t)
                for j in range(4):
                    if j == 1:
                        pe.wait_ge(pt_dve, 3 * t + e + 1)
                    if j == 2:
                        pe.wait_ge(pt_act, 5 * t + 2 * e + 2)
                    mm = nc.tensor.matmul(out[:, P * j:TP], vp[:, b, j, TS * e:TS * e + TS],
                                          pt[:, e, PTOFF[j]:PTOFF[j] + TP - P * j], start=j == 0, stop=j == 3)
                mm.then_inc(av_done, 1)

            def values_sample(t, b):
                pe.wait_ge(p_ready, 9 * t + 9)
                pe.wait_ge(pt_dve, 3 * t + 2)
                pe.wait_ge(pt_act, 5 * t + 4)
                nc.tensor.transpose(ps[:, 4, 0:P], sc_s[:, 0:PAST], ident).then_inc(pt_done, 1)
                nc.tensor.transpose(ps[0:TS, 3, 0:P], sc_s[:, PAST:], ident).then_inc(pt_done, 1)
                pe.wait_ge(pt_act, 5 * t + 5)
                pe.wait_ge(pt_dve, 3 * t + 3)
                for e in range(2):
                    c = slice(TS * e, TS * e + TS)
                    nc.tensor.matmul(ps[c, 6, 0:TS], vp[:, b, 5, c], pts[:, 0, c], start=True, stop=False)
                    mm = nc.tensor.matmul(ps[c, 6, 0:TS], vp[0:TS, b, 4, c], pts[0:TS, 1, c], start=False, stop=True)
                mm.then_inc(av_done, 1)

            def fox_pair(t, b, rounds, start=False, last=False):
                pe.wait_ge(max_ready, 9 * t + 4)
                scores_head(t, b, 1)
                scores_sample(t, b)
                values_head(t, b, 0, start)
                if not last:
                    pe.wait_ge(max_ready, 9 * t + 9)
                    cached_keys(t + 1, 1 - b, rounds + b)
                    scores_head(t + 1, 1 - b, 0)
                values_head(t, b, 1, start)
                values_sample(t, b)

            pe.wait_ge(taken, first["q"] + KD)
            cached_keys(0, 0, 1)
            scores_head(0, 0, 0)
            for b in range(2):
                fox_pair(b, b, 1, b == 0)
            with pe.Fori(1, PAIRS // 2 - 1) as i:
                for b in range(2):
                    fox_pair(2 * i + b, b, i + 1)
            for b in range(2):
                fox_pair(PAIRS - 2 + b, b, PAIRS // 2, last=b == 1)

            units("fox_out", xh, xl, lambda k: pe.wait_ge(fox_ready, 2 * k + 2))
            ffn("ffn2_1")
            sum_partitions()
            pe.wait_ge(y_ready, KD)
            for t in range(TT):
                r = ROWS[t]
                for a in range(2):
                    if t >= 2:
                        pe.wait_ge((ytok_act, ytok_dve)[a], t - 1)
                    for c in range(4):
                        mm = nc.tensor.transpose(ps[0:r, 4 + 2 * (t % 2) + a, P * c:P * c + P],
                                                 yT[:, 4 * a + c, P * t:P * t + r], ident)
                    mm.then_inc(yt_done, 1)


_INS = ["x_prompt", "x_sample", "state_ret", "cache_k", "cache_v", "cache_logf", "ffn1_g", "ffn1_w_in", "ffn1_w_out",
        "mix_g", "ffn2_g", "ffn2_w_in", "ffn2_w_out", "ret_w_in", "ret_gn_g", "ret_w_out", "kv_g", "fox_w_kvf",
        "fox_b_f", "fox_w_q", "fox_w_out", "final_g"]
_OUTS = [("y_prompt", (1, TP, D)), ("y_sample", (1, TS, D)), ("state_ret_prompt", (1, 1, HEADS, DK, DV)),
         ("k_prompt", (1, TP, FOX_HEADS, 64)), ("v_prompt", (1, TP, FOX_HEADS, 64)), ("logf_prompt", (1, TP, FOX_HEADS)),
         ("state_ret_sample", (1, 1, HEADS, DK, DV)), ("k_sample", (1, TS, FOX_HEADS, 64)),
         ("v_sample", (1, TS, FOX_HEADS, 64)), ("logf_sample", (1, TS, FOX_HEADS))]


def kernel(**inputs):
    import concourse.bacc as _bacc
    from concourse.bass_utils import run_bass_kernel_spmd as _run

    nc = _bacc.Bacc("TRN2", target_bir_lowering=False, num_devices=1)
    tables, mask = constant_tables()
    arrays = {name: np.ascontiguousarray(inputs[name]) for name in _INS}
    arrays |= {"tables": tables, "decay_mask": mask}
    ins = {name: nc.dram_tensor(f"in_{name}", a.shape, mybir.dt.from_np(a.dtype), kind="ExternalInput").ap()
           for name, a in arrays.items()}
    outs = {name: nc.dram_tensor(f"out_{name}", shape, F32, kind="ExternalOutput").ap() for name, shape in _OUTS}
    encoder(nc, ins, outs)
    r = _run(nc, [{f"in_{name}": a for name, a in arrays.items()}], core_ids=[0])
    return tuple(r.results[0][f"out_{name}"] for name, _ in _OUTS)
```
